# Optimizing a Trainium2 kernel written in Bass

```python
import jax, jax.numpy as jnp
from jax import lax
import numpy as np

D_MODEL = 1024
BATCH = 1
SEQ = 512
DEPTH = 1

N_META = 16
D_CONV = D_MODEL
CONV_WIDTH = 31
D_RNN = D_MODEL
RNN_HEAD_DIM = 128
N_RNN_HEADS = D_RNN // RNN_HEAD_DIM
CHUNK = 128
CHUNK_PAD = CHUNK - N_META
N_EXPERTS = 32
TOP_K = 4
D_FF = D_MODEL
SWIGLU_LIMIT = 7.0
SWIGLU_ALPHA = 1.702
EXPERT_BLOCK = 128
RMS_EPS = 1e-6
LN_EPS = 1e-5
IN_SIZES = (D_CONV, D_CONV, D_RNN, D_RNN, D_RNN, D_RNN, D_MODEL, D_MODEL)
D_IN = sum(IN_SIZES)

kernel_name = "hybrid_conformer_hgrn2_moe_block"

def rmsnorm(x, g):
    xf = x.astype(jnp.float32)
    y = xf * lax.rsqrt(jnp.mean(xf * xf, axis=-1, keepdims=True) + RMS_EPS)
    return (y * g.astype(jnp.float32)).astype(x.dtype)

def layernorm(x, g, b):
    xf = x.astype(jnp.float32)
    mu = jnp.mean(xf, axis=-1, keepdims=True)
    xc = xf - mu
    var = jnp.mean(xc * xc, axis=-1, keepdims=True)
    y = xc * lax.rsqrt(var + LN_EPS) * g.astype(jnp.float32) + b.astype(jnp.float32)
    return y.astype(x.dtype)

def conformer_conv_branch(zv, zg, w_dw, b_dw, ln_g, ln_b, w_out, b_out):
    a = zv * jax.nn.sigmoid(zg)
    kern = w_dw.astype(a.dtype)[:, None, :]
    a = lax.conv_general_dilated(a, kern, window_strides=(1,), padding=[(CONV_WIDTH - 1, 0)],
                                 dimension_numbers=('NWC', 'WIO', 'NWC'),
                                 feature_group_count=D_CONV) + b_dw
    a = jax.nn.silu(layernorm(a, ln_g, ln_b))
    return a @ w_out + b_out

def hgrn2_chunk_scan(q, k, v, logf):
    Bsz, N, H, dk = q.shape
    dv = v.shape[-1]
    nC = N // CHUNK

    def to_chunks(t):
        return t.reshape(Bsz, nC, CHUNK, H, t.shape[-1]).transpose(1, 0, 3, 2, 4)

    causal = jnp.tril(jnp.ones((CHUNK, CHUNK), dtype=bool))[None, None, :, :, None]

    def step(S, inp):
        qc, kc, vc, lfc = inp
        b = jnp.cumsum(lfc, axis=-2)
        inter = jnp.einsum('bhtd,bhdv->bhtv', qc * jnp.exp(b), S)
        diff = b[:, :, :, None, :] - b[:, :, None, :, :]
        decay = jnp.exp(jnp.where(causal, diff, -jnp.inf))
        scores = jnp.einsum('bhtd,bhtsd,bhsd->bhts', qc, decay, kc)
        intra = jnp.einsum('bhts,bhsv->bhtv', scores, vc)
        b_last = b[:, :, -1:, :]
        S_new = jnp.exp(b_last[:, :, 0, :])[..., None] * S + \
            jnp.einsum('bhsd,bhsv->bhdv', kc * jnp.exp(b_last - b), vc)
        return S_new, inter + intra

    S0 = jnp.zeros((Bsz, H, dk, dv), jnp.float32)
    _, ys = lax.scan(step, S0, (to_chunks(q), to_chunks(k), to_chunks(v), to_chunks(logf)))
    return ys.transpose(1, 0, 3, 2, 4).reshape(Bsz, N, H, dv)

def hgrn2_branch(zq, zf, zi, zg, lb, g_onorm, w_out):
    Bsz, L = zq.shape[:2]

    def heads(t):
        return t.reshape(Bsz, L, N_RNN_HEADS, RNN_HEAD_DIM).astype(jnp.float32)

    lbh = lb.astype(jnp.float32).reshape(N_RNN_HEADS, RNN_HEAD_DIM)
    q = jax.nn.silu(heads(zq))
    f = lbh + (1.0 - lbh) * jax.nn.sigmoid(heads(zf))
    logf = jnp.log(f)
    v = heads(zi)
    pad = ((0, 0), (CHUNK_PAD, 0), (0, 0), (0, 0))
    q, v, logf = jnp.pad(q, pad), jnp.pad(v, pad), jnp.pad(logf, pad)
    k = -jnp.expm1(logf)
    o = hgrn2_chunk_scan(q, k, v, logf)[:, CHUNK_PAD:]
    o = o * lax.rsqrt(jnp.mean(o * o, axis=-1, keepdims=True) + RMS_EPS)
    o = o * g_onorm.astype(jnp.float32).reshape(N_RNN_HEADS, RNN_HEAD_DIM)
    o = o.reshape(Bsz, L, D_RNN).astype(zg.dtype) * jax.nn.silu(zg)
    return o @ w_out

def mixer_block(u, lb, w_in, w_dw, b_dw, ln_g, ln_b, w_conv_out, b_conv_out,
                g_onorm, w_rnn_out, w_o):
    z = u @ w_in
    split_points = np.cumsum(IN_SIZES)[:-1].tolist()
    zc_v, zc_g, zq, zf, zi, zg, ga, gb = jnp.split(z, split_points, axis=-1)
    a = conformer_conv_branch(zc_v, zc_g, w_dw, b_dw, ln_g, ln_b, w_conv_out, b_conv_out)
    r = hgrn2_branch(zq, zf, zi, zg, lb, g_onorm, w_rnn_out)
    y = jax.nn.sigmoid(ga) * a + jax.nn.sigmoid(gb) * r
    return y @ w_o

def moe_block(u, w_router, b_router, w_gu, b_gu, w_dn, b_dn):
    Bsz, L, D = u.shape
    T = Bsz * L
    TK = T * TOP_K
    xt = u.reshape(T, D)
    logits = (xt @ w_router + b_router).astype(jnp.float32)
    top_val, top_idx = lax.top_k(logits, TOP_K)
    gates = jax.nn.softmax(top_val, axis=-1)
    flat_e = top_idx.reshape(-1).astype(jnp.int32)
    flat_tok = jnp.arange(TK, dtype=jnp.int32) // TOP_K
    flat_w = gates.reshape(-1)
    order = jnp.argsort(flat_e)
    se, stok, sw = flat_e[order], flat_tok[order], flat_w[order]
    counts = jnp.bincount(flat_e, length=N_EXPERTS)
    starts = jnp.cumsum(counts) - counts
    padded = (counts + EXPERT_BLOCK - 1) // EXPERT_BLOCK * EXPERT_BLOCK
    pends = jnp.cumsum(padded)
    pstarts = pends - padded
    dest = pstarts[se] + (jnp.arange(TK, dtype=jnp.int32) - starts[se])
    n_blocks = -(-(TK + N_EXPERTS * (EXPERT_BLOCK - 1)) // EXPERT_BLOCK)
    n_slots = n_blocks * EXPERT_BLOCK
    slot_tok = jnp.full((n_slots,), T, jnp.int32).at[dest].set(stok)
    slot_w = jnp.zeros((n_slots,), jnp.float32).at[dest].set(sw)
    block_e = jnp.minimum(jnp.searchsorted(pends, jnp.arange(n_blocks) * EXPERT_BLOCK, side='right'),
                          N_EXPERTS - 1)
    x_pad = jnp.concatenate([xt, jnp.zeros((1, D), xt.dtype)], axis=0)
    xb = x_pad[slot_tok].reshape(n_blocks, EXPERT_BLOCK, D)

    def expert_block(args):
        xblk, e = args
        gu = xblk @ w_gu[e] + b_gu[e]
        gate, up = gu[:, :D_FF], gu[:, D_FF:]
        gate = jnp.minimum(gate, SWIGLU_LIMIT)
        up = jnp.clip(up, -SWIGLU_LIMIT, SWIGLU_LIMIT)
        hdn = (up + 1.0) * (gate * jax.nn.sigmoid(SWIGLU_ALPHA * gate))
        return hdn @ w_dn[e] + b_dn[e]

    yb = lax.map(expert_block, (xb, block_e)).reshape(n_slots, D)
    y = jnp.zeros((T + 1, D), u.dtype).at[slot_tok].add(yb * slot_w[:, None].astype(yb.dtype))
    return y[:T].reshape(Bsz, L, D)

def setup_inputs(seed: int = 0) -> dict:
    key = jax.random.key(seed)
    ks = jax.random.split(key, 24)
    f32 = jnp.float32

    def nrm(k, shape, scale):
        return jax.random.normal(k, shape, f32) * scale

    def gain(k, shape):
        return 1.0 + 0.02 * jax.random.normal(k, shape, f32)

    return {
        "x": nrm(ks[0], (BATCH, SEQ, D_MODEL), 1.0),
        "meta_tokens": nrm(ks[1], (N_META, D_MODEL), 1.0),
        "lb_logits": nrm(ks[2], (DEPTH + 1, D_RNN), 0.1),
        "g_mix": gain(ks[3], (DEPTH, D_MODEL)),
        "w_in": nrm(ks[4], (DEPTH, D_MODEL, D_IN), D_MODEL ** -0.5),
        "w_dw": nrm(ks[5], (DEPTH, CONV_WIDTH, D_CONV), CONV_WIDTH ** -0.5),
        "b_dw": nrm(ks[6], (DEPTH, D_CONV), 0.02),
        "ln_g": gain(ks[7], (DEPTH, D_CONV)),
        "ln_b": nrm(ks[8], (DEPTH, D_CONV), 0.02),
        "w_conv_out": nrm(ks[9], (DEPTH, D_CONV, D_MODEL), D_CONV ** -0.5),
        "b_conv_out": nrm(ks[10], (DEPTH, D_MODEL), 0.02),
        "g_onorm": gain(ks[11], (DEPTH, D_RNN)),
        "w_rnn_out": nrm(ks[12], (DEPTH, D_RNN, D_MODEL), D_RNN ** -0.5),
        "w_o": nrm(ks[13], (DEPTH, D_MODEL, D_MODEL), D_MODEL ** -0.5),
        "g_ffn": gain(ks[14], (DEPTH, D_MODEL)),
        "w_router": nrm(ks[15], (DEPTH, D_MODEL, N_EXPERTS), D_MODEL ** -0.5),
        "b_router": nrm(ks[16], (DEPTH, N_EXPERTS), 0.01),
        "w_gate_up": nrm(ks[17], (DEPTH, N_EXPERTS, D_MODEL, 2 * D_FF), D_MODEL ** -0.5),
        "b_gate_up": nrm(ks[18], (DEPTH, N_EXPERTS, 2 * D_FF), 0.02),
        "w_down": nrm(ks[19], (DEPTH, N_EXPERTS, D_FF, D_MODEL), D_FF ** -0.5),
        "b_down": nrm(ks[20], (DEPTH, N_EXPERTS, D_MODEL), 0.02),
        "g_final": gain(ks[21], (D_MODEL,)),
    }

def reference(x, meta_tokens, lb_logits, g_mix, w_in, w_dw, b_dw, ln_g, ln_b, w_conv_out,
              b_conv_out, g_onorm, w_rnn_out, w_o, g_ffn, w_router, b_router, w_gate_up,
              b_gate_up, w_down, b_down, g_final):
    Bsz = x.shape[0]
    meta = jnp.broadcast_to(meta_tokens.astype(x.dtype)[None], (Bsz, N_META, x.shape[-1]))
    h = jnp.concatenate([meta, x], axis=1)
    lower_bounds = jnp.cumsum(jax.nn.softmax(lb_logits.astype(jnp.float32), axis=0), axis=0)
    for l in range(DEPTH):
        h = h + mixer_block(rmsnorm(h, g_mix[l]), lower_bounds[l], w_in[l], w_dw[l], b_dw[l],
                            ln_g[l], ln_b[l], w_conv_out[l], b_conv_out[l], g_onorm[l],
                            w_rnn_out[l], w_o[l])
        h = h + moe_block(rmsnorm(h, g_ffn[l]), w_router[l], b_router[l], w_gate_up[l],
                          b_gate_up[l], w_down[l], b_down[l])
    return rmsnorm(h, g_final)[:, N_META:]


_drawn_inputs = setup_inputs


def setup_inputs(seed=0):
    import zlib

    import numpy as np

    out = dict(_drawn_inputs(seed))
    spreads = {}
    factors = {'lb_logits': 2.763, 'b_gate_up': 5.512, 'b_down': 6.284, 'g_final': 2.748}
    for name, (base, spread) in spreads.items():
        noise = np.random.default_rng([zlib.crc32(name.encode()), seed]).standard_normal(out[name].shape)
        drawn = base * np.exp(spread * noise) if base else spread * noise
        out[name] = __import__('jax').numpy.asarray(drawn.astype(out[name].dtype))
    for name, factor in factors.items():
        out[name] = (out[name] * factor).astype(out[name].dtype)
    return out
```

```python
from contextlib import ExitStack

import concourse.bass as bass
from concourse import mybir

ALU = mybir.AluOpType
ACT = mybir.ActivationFunctionType
AX_X = mybir.AxisListType.X
F32 = mybir.dt.float32
F32R = mybir.dt.float32r
F16 = mybir.dt.float16
I32 = mybir.dt.int32
U32 = mybir.dt.uint32
ds = bass.ds

P = 128
D = 1024
KD = D // P
SEQ = 512
NT = SEQ // P
META = 16
TOK = SEQ + META
HALF = TOK // 2
HEADS = 8
TAPS = 31
PADL = TAPS - 1 - META
NP_ROWS = TAPS + 8
R_BDW, R_GMIX, R_LNG, R_LNB, R_BCO, R_GON, R_LB = 31, 32, 33, 34, 35, 36, 37
LEVELS = (64, 32, 16, 8, 4, 2, 1)
NL = len(LEVELS)
E = 32
TOPK = 4
FF = 1024
ROWS = SEQ * TOPK
SLOTS = 96
PASSES = -(-SEQ // SLOTS)
PAD = 5000.0
RMS_EPS = 1e-6
LN_EPS = 1e-5
LIMIT = 7.0
ALPHA = 1.702
G_CV, G_CG, G_Q, G_F, G_I, G_OG, G_GA, G_GB = range(8)
UNITS = (G_I, G_F, G_Q, G_CG, G_CV, G_GA, G_GB, G_OG)
NU = len(UNITS)
MW = 4
MIX_U = HEADS * NU
STEPS = TAPS + 1
GU_U, DN_U = 8, 4
STEP_U = GU_U + DN_U
RAW = 12
SPL = 4
PASS_U = E * STEP_U


def hybrid_block(nc, x, meta_tokens, lb_logits, g_mix, w_in, w_dw, b_dw, ln_g, ln_b, w_conv_out,
                 b_conv_out, g_onorm, w_rnn_out, w_o, g_ffn, w_router, b_router, w_gate_up,
                 b_gate_up, w_down, b_down, g_final, out):
    ctx = ExitStack()
    with ctx:
        BASE = 16512
        cursor = [BASE]

        def at(name, shape, dt, offset):
            return nc.alloc_sbuf_tensor_at(name, [P, *shape], dt, offset=offset)

        def size(shape, width=4):
            n = width
            for s in shape:
                n *= s
            return (n + 31) // 32 * 32

        def place(name, shape, dt=F32, width=4):
            t = at(name, shape, dt, cursor[0])
            cursor[0] += size(shape, width)
            return t

        ident = place("ident", [P])
        ones = place("ones", [P])
        ones_d = place("ones_over_d", [P])
        ones_h = place("ones_over_head", [P])
        tri = place("strictly_before", [P])
        PT = place("params_fm", [NP_ROWS * KD])
        lbw = place("lower_bound_work", [KD, 4])
        lb = place("lower_bound", [KD])
        omlb = place("one_minus_lb", [KD])
        neg_omlb = place("minus_one_minus_lb", [KD])
        ss = place("sum_squares", [8])
        rstd = place("rstd", [8])
        wr = place("w_router_sb", [KD, E])
        br_bc = place("b_router_bc", [E])
        eps_rms = place("eps_rms", [1])
        eps_ln = place("eps_ln", [1])
        iota_e = place("iota_expert", [E])
        iota_s = place("iota_slot", [P])
        tok1 = place("four_tokens_plus_one", [NT])
        logits = place("logits", [NT, E])
        top_v = place("top_values", [NT, 8])
        top_i = place("top_indices", [NT, 8], U32)
        top_f = place("top_indices_f", [NT, TOPK])
        gex = place("gate_exp", [NT, TOPK])
        gsum = place("gate_sum", [NT])
        gates = place("gates", [NT, TOPK])
        oneh = place("one_hot", [NT, TOPK, E])
        member = place("member", [NT, E])
        choice = place("choice", [NT, E])
        rankm = place("rank_of_members", [NT, E])
        cmax = place("count_max", [1])
        cmax_i = place("count_max_i", [1], I32)
        slot_eq = place("slot_is_empty", [E])
        slot_f = place("slot_row_f", [E])
        scat_i = place("scatter_rows", [E], I32)
        gath_i = place("gather_rows", [E], I32)
        scat_c = place("scatter_rows_now", [1], I32)
        gath_c = place("gather_rows_now", [1], I32)
        selbase = place("select_base", [E])
        sel_g = place("select_gate_up", [P], F32R)
        sel_d = place("select_down", [P], F32R)
        aval = place("row_plus_one", [NT, E], F16, 2)

        W0 = cursor[0]
        C0 = W0 + 32768
        U0 = C0 + 65536
        B0 = U0 + 2 * KD * TOK * 4
        SLOT = KD * P * 4
        wm = [at(f"mixer_weights{i}", [KD, P], F32, W0 + i * SLOT) for i in range(MW)]
        wm_lo = [at(f"mixer_weights_lo{i}", [KD, P], F32R, W0 + i * SLOT) for i in range(MW)]
        wm_hi = [at(f"mixer_weights_hi{i}", [KD, P], F32R, W0 + (MW + i) * SLOT) for i in range(MW)]
        conv = at("conv_out_fm", [KD * SEQ], F32, C0)
        act_lo = at("conv_act_lo", [KD * SEQ], F32R, C0)
        sg_a = at("sigmoid_gate_a", [KD * SEQ], F32, C0 + 16384)
        sg_b = at("sigmoid_gate_b", [KD * SEQ], F32, C0 + 32768)
        mixed_lo = at("mixed_lo", [KD * SEQ], F32R, C0 + 32768)
        r_fm = at("rnn_fm", [KD * SEQ], F32, C0 + 49152)
        r_lo = at("rnn_lo", [KD * SEQ], F32R, C0 + 49152)
        u_hi = at("u_hi", [KD, TOK], F32R, U0)
        u_fm = at("u_fm", [KD, TOK], F32, U0 + KD * TOK * 4)
        u_lo = at("u_lo", [KD, TOK], F32R, U0 + KD * TOK * 4)

        cursor[0] = B0
        D_l = place("level_decay", [NL, SEQ])
        sf = place("sig_f", [TOK])
        lf = place("log_f", [TOK])
        kk = place("k_fm", [TOK])
        vv = place("v_fm", [TOK])
        qq = place("q_fm", [SEQ])
        gg = place("out_gate", [SEQ])
        tq = place("sigmoid_q", [SEQ])
        tc = place("sigmoid_conv", [TOK])
        tg = place("sigmoid_out_gate", [SEQ])
        bb = place("log_decay", [TOK])
        eb = place("decay_from_start", [SEQ])
        ke = place("decay_to_end", [META + 3 * P])
        qb = place("q_decayed", [SEQ])
        kd = place("k_decayed", [META + 3 * P])
        vt = place("v_tm", [5, P])
        kt = place("k_decayed_tm", [4, P])
        S = place("states", [NT, P])
        rs = place("o_squared_then_scale", [SEQ])
        o_rstd = place("o_rstd", [NT])
        conv_odd = place("conv_odd_taps", [SEQ])
        ap_ = place("conv_in", [PADL + TOK])
        ST = place("scores_t", [NT, P])
        keep = place("chunk_reset", [TOK])
        masks = place("level_masks", [NL, P // 2])
        END = max(cursor[0], B0 + 51200 + 16384)
        assert END <= 229344, END
        x_sb = at("x_sb", [NT, D], F32, B0)
        m_sb = at("meta_sb", [D], F32, B0 + 16384)
        rows = at("param_rows", [D], F32, B0 + 20480)
        junk = at("square_junk", [D], F32, B0 + 24576)
        r_hi = at("rnn_hi", [KD * SEQ], F32R, U0)
        mixed_hi = at("mixed_hi", [KD * SEQ], F32R, C0 + 16384)
        sq_ln = at("ln_squares", [KD, SEQ], F32, B0 + 16384)
        act_hi = at("conv_act_hi", [KD * SEQ], F32R, B0 + 16384)
        aa = at("mixed_a", [2, SEQ], F32, B0 + 32768)
        rstd_ln = at("ln_rstd", [SEQ], F32, B0 + 40960)
        ysig = at("ln_sigmoid", [2, SEQ], F32, B0 + 43008)
        gffn_bc = at("g_ffn_bc", [D], F32, B0 + 43008)
        wo_at = (U0 + 16384, U0)
        wo = [at(f"w_o_half{j}", [KD, D // 2], F32, o) for j, o in enumerate(wo_at)]
        wo_lo = [at(f"w_o_lo{j}", [KD, D // 2], F32R, o) for j, o in enumerate(wo_at)]
        wo_hi = [at(f"w_o_hi{j}", [KD, D // 2], F32R, o) for j, o in enumerate((B0 + 51200, B0))]
        h_sb = at("h_tm", [NT, D], F32, C0 + 49152)
        u2 = at("u2_tm", [NT, D], F32, B0 + 16384)
        u2t = at("u2_fm", [2, KD, P], F32, B0 + 32768)
        slot_ohs = [at(f"slot_one_hot{i}", [E, P], F16, W0 + 8192 * i) for i in range(NT)]
        raw_at = [C0, C0 + 8192] + [U0 + 8192 * i for i in range(4)] + [C0 + 8192 * i for i in (2, 3)] + [
            B0 + 32768 + 8192 * i for i in range(2)] + [C0 + 8192 * i for i in (4, 5)]
        raw = [at(f"raw_weights{i}", [2 * D], F32, o) for i, o in enumerate(raw_at)]
        w_lo = [at(f"weights_lo{i}", [2 * D], F32R, o) for i, o in enumerate(raw_at)]
        w_hi = at("weights_hi", [SPL, 2 * D], F32R, B0)
        b_raw = at("bias_raw", [3 * D], F32, C0 + 32768)
        b_hl = at("bias_hi_lo", [3 * D], F32R, B0 + 49152)
        xe = at("expert_rows", [D], F32, B0 + 61440)
        xt_hi = at("expert_rows_t_hi", [KD, P], F32R, W0)
        xt_lo = at("expert_rows_t_lo", [KD, P], F32R, W0 + 4096)
        ht_hi = at("hidden_t_hi", [KD, P], F32R, W0 + 8192)
        ht_lo = at("hidden_t_lo", [KD, P], F32R, W0 + 12288)
        g_act = at("gate_act", [FF], F32, W0 + 16384)
        g_sig = at("gate_sigmoid", [FF], F32, W0 + 20480)
        u_act = at("up_act", [FF], F32, W0 + 24576)
        y_sb = at("expert_out", [D], F32, W0 + 28672)
        y4 = [at(f"chosen_outputs{i}", [TOPK, D], F32, o) for i, o in
              enumerate((U0, U0 + 16384, C0, C0 + 16384))]
        fin = at("final_rows", [NT, D], F32, B0)
        junk3 = at("square_junk3", [D], F32, B0 + 16384)
        gfin_bc = at("g_final_bc", [D], F32, B0 + 20480)
        gate_diag = at("gate_diagonals", [NT, 2, P], F32, B0 + 24576)

        ps = ctx.enter_context(nc.psum_tensor("ps", [P, 8, 512], F32))
        Z = [ps[:, 0:2, :], ps[:, 2:4, :]]
        SC = [ps[:, 4, :], ps[:, 5, :]]
        HB = [ps[:, 6, :], ps[:, 7, :]]

        u2_dram = nc.dram_tensor("u2_rows", [SEQ, D], F32, kind="Internal").ap()
        y_dram = nc.dram_tensor("y_rows", [ROWS, D], F32, kind="Internal").ap()

        sems = {}

        def sem(name):
            if name not in sems:
                sems[name] = ctx.enter_context(nc.semaphore(name))
            return sems[name]

        x_landed = [sem(f"x_landed{i}") for i in range(NT + 1)]
        w_landed = [sem(f"mixer_w_landed{u}") for u in range(MW)]
        raw_landed = [sem(f"raw_landed{s}") for s in range(RAW)]
        y4_landed = [[sem(f"y4_landed{i}"), sem(f"y4_landed{i}" + ("" if i in (1, 2) else "_choices23"))] for i in range(NT)]

        x_d = x[0].rearrange("(i p) d -> p i d", p=P)
        out_d = out[0].rearrange("(i p) d -> p i d", p=P)
        w_in_d = w_in[0].rearrange("(k p) n -> p k n", p=P)
        w_last_d = [w[0].rearrange("(k p) n -> p k n", p=P) for w in (w_rnn_out, w_conv_out)]
        y_rows_d = y_dram.rearrange("(i p k) d -> i p k d", p=P, k=TOPK)

        def cols(t, h, n=SEQ):
            return t[:, ds(h * n, n)]

        def lvl(t, m):
            return t.rearrange("p (b two m) -> p b two m", two=2, m=m)

        block = ctx.enter_context(nc.Block())

        def wait_alone(eng, s, value):
            eng.wait_ge(s, value)
            eng.sem_inc(sem("waits_over"), 1)

        def more_passes(eng, one_pass):
            eng.wait_ge(sem("count_ready"), 1)
            most = eng.value_load(cmax_i[0:1, 0:1], min_val=1, max_val=SEQ)
            with eng.Fori(1, PASSES) as r:
                with eng.If(most > r * SLOTS):
                    one_pass(r)

        @block.sync
        def _(sp):
            def load_x(i):
                sp.dma_start(x_sb[:, i, :], x_d[:, i]).then_inc(x_landed[i], 16)

            load_x(0)
            load_x(1)
            for r, src in ((0, w_dw[0]), (R_BDW, b_dw), (R_GMIX, g_mix), (R_LNG, ln_g),
                           (R_LNB, ln_b), (R_BCO, b_conv_out), (R_GON, g_onorm), (R_LB, lb_logits)):
                n = src.shape[0]
                sp.dma_start(rows[r:r + n, :], src).then_inc(sem("rows_landed"), 16)
            load_x(2)
            load_x(3)
            sp.dma_start(m_sb[0:META, :], meta_tokens).then_inc(x_landed[NT], 16)
            def load_mixer(n, s, src):
                if not isinstance(n, int):
                    wait_alone(sp, sem("unit_done"), n - MW + 1)
                elif n >= MW:
                    sp.wait_ge(sem("unit_done"), n - MW + 1)
                sp.dma_start(wm[s % MW][:], src).then_inc(w_landed[s % MW], 16)

            for u in range(NU):
                load_mixer(u, u, w_in_d[:, :, UNITS[u] * D:UNITS[u] * D + P])
                if u == MW - 1:
                    sp.dma_start(wr[:], w_router[0].rearrange("(k p) e -> p k e", p=P)).then_inc(sem("consts_landed"), 16)
                    sp.dma_start(br_bc[:], b_router.to_broadcast([P, E])).then_inc(sem("consts_landed"), 16)
            with sp.Fori(1, HEADS) as h:
                for u in range(NU):
                    load_mixer(h * NU + u, u, w_in_d[:, :, ds(UNITS[u] * D + h * P, P)])

            def load_unit(n, slot, src):
                if not isinstance(n, int) or n >= RAW:
                    wait_alone(sp, sem("unit_used"), n - RAW + 1)
                sp.dma_start(raw[slot][:] if len(src.shape) == 2 else
                             raw[slot].rearrange("p (j c) -> p j c", j=2), src).then_inc(raw_landed[slot], 16)

            def gu_src(e, u):
                return w_gate_up[0, ds(e, 1), u * P:(u + 1) * P, :].rearrange("o p n -> (o p) n")

            def dn_src(e, v):
                return w_down[0, ds(e, 1), 2 * v * P:2 * (v + 1) * P, :].rearrange("o (j p) n -> (o p) j n", p=P)

            wo_d = w_o[0].rearrange("(k p) n -> p k n", p=P)
            for n, w_d in enumerate(w_last_d):
                for j in range(KD):
                    load_mixer(MIX_U + n * KD + j, j, w_d[:, :, j * P:(j + 1) * P])
                    if (n, j) == (0, 3):
                        sp.wait_ge(sem("unit_done"), MIX_U)
                        sp.dma_start(wo[0][:], wo_d[:, :, 0:D // 2]).then_inc(sem("wo_landed0"), 16)
                    if (n, j) == (1, 3):
                        sp.wait_ge(sem("unit_done"), MIX_U + KD)
                        sp.dma_start(wo[1][:], wo_d[:, :, D // 2:D]).then_inc(sem("wo_landed1"), 16)
                        sp.dma_start(h_sb[:], x_d).then_inc(sem("h_landed"), 16)
            sp.wait_ge(sem("act_ready"), KD)
            sp.dma_start(gffn_bc[:], g_ffn.to_broadcast([P, D])).then_inc(sem("consts_landed"), 16)
            sp.wait_ge(sem("unit_done"), MIX_U + 2 * KD)
            for u in range(2):
                load_unit(u, u, gu_src(0, u))
            sp.wait_ge(sem("wo_done"), 2 * NT)
            for c in range(2):
                sp.dma_start(b_raw[E * c:E * c + E, 0:2 * D], b_gate_up[0]).then_inc(sem("bias_landed"), 16)
                sp.dma_start(b_raw[E * c:E * c + E, 2 * D:3 * D], b_down[0]).then_inc(sem("bias_landed"), 16)
            for u in range(2, 8):
                load_unit(u, u, gu_src(0, u))
            sp.wait_ge(sem("logits_done"), NT)
            for u in range(2):
                load_unit(GU_U + u, GU_U + u, gu_src(1, u))
            sp.wait_ge(sem("bias_lo"), 1)
            sp.wait_ge(sem("gathered"), 16)

            def weights(r):
                base = r * PASS_U
                for u in range(GU_U if isinstance(r, int) else 0, GU_U):
                    load_unit(base + u, u % RAW, gu_src(0, u))
                if isinstance(r, int):
                    for u in range(2, RAW - GU_U):
                        load_unit(GU_U + u, GU_U + u, gu_src(1, u))
                    for u in range(RAW - GU_U, STEP_U):
                        load_unit(GU_U + u, (GU_U + u) % RAW, gu_src(1, u) if u < GU_U else dn_src(0, u - GU_U))
                with sp.Fori(2 if isinstance(r, int) else 1, E) as e:
                    for u in range(STEP_U):
                        n = e * STEP_U + (base - DN_U + u)
                        src = gu_src(e, u) if u < GU_U else dn_src(e - 1, u - GU_U)
                        load_unit(n, (GU_U + u) % RAW, src)
                for v in range(DN_U):
                    load_unit(base + PASS_U - DN_U + v, (PASS_U - DN_U + v) % RAW, dn_src(E - 1, v))

            weights(0)
            more_passes(sp, weights)
            sp.wait_ge(sem("all_scattered"), 1)
            for i in range(NT):
                if i in (1, 2):
                    sp.dma_start(y4[i][:], y_rows_d[i]).then_inc(y4_landed[i][0], 16)
                else:
                    for b in range(2):
                        sp.dma_start(y4[i][:, 2 * b:2 * b + 2], y_rows_d[i][:, 2 * b:2 * b + 2]).then_inc(y4_landed[i][b], 16)
                if i == 1:
                    sp.dma_start(gfin_bc[:], g_final.unsqueeze(0).to_broadcast([P, D])).then_inc(sem("g_final_landed"), 16)
            for i in range(NT):
                sp.wait_ge(sem("final_ready"), i + 1)
                sp.dma_start(out_d[:, i], fin[:, i]).then_inc(sem("stored"), 16)
            sp.wait_ge(sem("stored"), 16 * NT)

        @block.gpsimd
        def _(pool):
            g = nc.gpsimd
            g.memset(ones[:], 1.0).then_inc(sem("c_ones"), 1)
            g.memset(ones_d[:], 1.0 / D).then_inc(sem("c_ones"), 1)
            g.memset(eps_rms[:], RMS_EPS)
            g.memset(eps_ln[:], LN_EPS)
            g.memset(ones_h[:], 1.0 / P).then_inc(sem("c_ones"), 1)
            g.memset(masks[:], 1.0).then_inc(sem("c_ones"), 1)
            pool.wait_ge(sem("c_ones"), 4)
            g.affine_select(out=ident[:], in_=ones[:], compare_op=ALU.is_equal, fill=0.0, base=0,
                            pattern=[[-1, P]], channel_multiplier=1).then_inc(sem("c_ident"), 1)
            g.affine_select(out=tri[:], in_=ones[:], compare_op=ALU.is_gt, fill=0.0, base=0,
                            pattern=[[1, P]], channel_multiplier=-1).then_inc(sem("c_ident"), 1)
            g.memset(ap_[:, 0:PADL], 0.0)
            g.memset(ST[:], 0.0)
            g.memset(keep[:], 1.0).then_inc(sem("c_keep"), 1)
            pool.wait_ge(sem("c_keep"), 1)
            g.memset(keep[:, 0:1], 0.0)
            g.memset(keep[:, META:TOK:P], 0.0).then_inc(sem("c_keep"), 1)
            for n, m in enumerate(LEVELS):
                v = masks[:, n, :]
                pat = [[-2 * m, P // (2 * m)], [0, m]]
                g.affine_select(out=v, in_=v, compare_op=ALU.is_ge, fill=0.0, base=0,
                                pattern=pat, channel_multiplier=1).then_inc(sem("c_mask"), 1)
                pool.wait_ge(sem("c_mask"), 2 * n + 1)
                pat = [[2 * m, P // (2 * m)], [0, m]]
                g.affine_select(out=v, in_=v, compare_op=ALU.is_ge, fill=0.0, base=m - 1,
                                pattern=pat, channel_multiplier=-1).then_inc(sem("c_mask"), 1)
            g.iota(iota_e[:], pattern=[[1, E]], base=0, channel_multiplier=0,
                   allow_small_or_imprecise_dtypes=True)
            g.iota(iota_s[:], pattern=[[1, P]], base=0, channel_multiplier=0,
                   allow_small_or_imprecise_dtypes=True)
            g.iota(tok1[:], pattern=[[TOPK * P, NT]], base=1, channel_multiplier=TOPK,
                   allow_small_or_imprecise_dtypes=True)
            g.memset(selbase[:], 0.0).then_inc(sem("c_sel"), 1)
            pool.wait_ge(sem("c_sel"), 1)
            g.affine_select(out=selbase[:], in_=selbase[:], compare_op=ALU.not_equal, fill=1.0, base=0,
                            pattern=[[-1, E]], channel_multiplier=1).then_inc(sem("c_sel"), 1)
            pool.wait_ge(sem("c_sel"), 2)
            g.affine_select(out=selbase[:], in_=selbase[:], compare_op=ALU.not_equal, fill=1.0, base=-E,
                            pattern=[[-1, E]], channel_multiplier=1).then_inc(sem("c_sel"), 1)

            for i in range(NT):
                pool.wait_ge(sem("u2_ready"), i + 1)
                g.dma_start(u2_dram[i * P:(i + 1) * P, :], u2[:, i, :]).then_inc(sem("u2_stored"), 16)
            pool.wait_ge(sem("u2_stored"), 16 * NT)
            g.engine_nop().then_inc(sem("u2_kept"), 1)
            pool.wait_ge(sem("wo_done"), 2 * NT)
            g.memset(xe[:], 0.0).then_inc(sem("xe_cleared"), 1)
            pool.wait_ge(sem("xe_cleared"), 1)

            def gather(e, n):
                g.tensor_copy(gath_c[0:SLOTS, :], gath_i[0:SLOTS, ds(e, 1)]).then_inc(sem("gath_now"), 1)
                wait_alone(pool, sem("gath_now"), n + 1)
                g.indirect_dma_start(out=xe[0:SLOTS, :], out_offset=None, in_=u2_dram[:, :],
                                     in_offset=bass.IndirectOffsetOnAxis(ap=gath_c[0:SLOTS, 0:1], axis=0),
                                     bounds_check=SEQ - 1, oob_is_err=False).then_inc(sem("gathered"), 16)

            def scatter(e, n):
                wait_alone(pool, sem("y_ready"), n + 1)
                g.tensor_copy(scat_c[0:SLOTS, :], scat_i[0:SLOTS, ds(e, 1)]).then_inc(sem("scat_now"), 1)
                wait_alone(pool, sem("scat_now"), n + 1)
                g.indirect_dma_start(out=y_dram[:, :],
                                     out_offset=bass.IndirectOffsetOnAxis(ap=scat_c[0:SLOTS, 0:1], axis=0),
                                     in_=y_sb[0:SLOTS, :], in_offset=None,
                                     bounds_check=ROWS - 1, oob_is_err=False).then_inc(sem("scattered"), 16)

            def moves(r):
                base = r * E
                wait_alone(pool, sem("table_ready"), r + 1)
                for e in range(4):
                    wait_alone(pool, sem("x_turned"), base + e)
                    gather(e, base + e)
                with pool.Fori(2, E - 2) as e:
                    scatter(e - 2, base + e - 2)
                    wait_alone(pool, sem("x_turned"), base + e + 2)
                    gather(e + 2, base + e + 2)
                for e in range(E - 4, E):
                    scatter(e, base + e)
                wait_alone(pool, sem("scattered"), 16 * (base + E))

            moves(0)
            more_passes(pool, moves)
            g.engine_nop().then_inc(sem("all_scattered"), 1)

        @block.tensor
        def _(pe):
            mm = pe.matmul

            def tr(out, in_):
                n = in_.shape[0]
                return pe.transpose(out, in_, ident[0:n, 0:n])

            pe.wait_ge(sem("c_ident"), 2)
            pe.wait_ge(sem("rows_landed"), 16 * 8)
            for k in range(KD):
                last = tr(ps[:, 7, k * NP_ROWS:(k + 1) * NP_ROWS], rows[0:NP_ROWS, k * P:(k + 1) * P])
            last.then_inc(sem("rows_turned"), 1)
            for i in range(NT):
                pe.wait_ge(sem("x_normed"), i + 1)
                if i >= 2:
                    pe.wait_ge(sem("u_ready"), i - 1)
                for k in range(KD):
                    last = tr(ps[:, 2 * (i % 2) + k // 4, (k % 4) * P:(k % 4 + 1) * P], x_sb[:, i, k * P:(k + 1) * P])
                last.then_inc(sem("x_t"), 1)
            pe.wait_ge(sem("x_normed"), NT + 1)
            for k in range(KD):
                last = tr(ps[:, 4, k * META:(k + 1) * META], m_sb[0:META, k * P:(k + 1) * P])
            last.then_inc(sem("x_t"), 1)

            ALL = (G_F, G_I, G_CG, G_CV)

            def z_unit(h, u):
                freed = [("z_out_act", 5 * h), ("z_out_dve", 3 * h), ("z_out_act", 5 * h + 1),
                         ("z_out_act", 5 * h + 2), ("z_out_dve", 3 * h + 1), ("z_out_act", 5 * h + 3),
                         ("z_out_dve", 3 * h + 2), ("z_out_act", 5 * h + 4)][u]
                pe.wait_ge(sem(freed[0]), freed[1])
                pe.wait_ge(sem("mixer_lo"), h * NU + u + 1)
                if UNITS[u] in ALL:
                    parts = [(Z[u % 2][:, c, 0:HALF], slice(c * HALF, (c + 1) * HALF)) for c in range(2)]
                else:
                    parts = [(Z[u % 2][:, 0, :], slice(META, TOK))]
                for k in range(KD):
                    for w, t in ((wm_hi, u_hi), (wm_hi, u_lo), (wm_lo, u_hi)):
                        for bank, tok in parts:
                            last = mm(bank, lhsT=w[u % MW][:, k, :], rhs=t[:, k, tok],
                                      start=k == 0 and w is wm_hi and t is u_hi,
                                      stop=k == KD - 1 and w is wm_lo)
                last.then_inc(sem("unit_done"), 1)

            def scores(g, n, bank, signal):
                for c in range(NT):
                    keys = D_l[:, n, c * P:(c + 1) * P]
                    last = mm(SC[bank][:, (n % 2) * 256 + c * 64:(n % 2) * 256 + (c + 1) * 64].rearrange(
                                  "p (b m) -> p b m", m=LEVELS[n]),
                              lhsT=keys, rhs=lvl(keys, LEVELS[n])[:, :, 1, :], start=True, stop=True)
                if signal:
                    last.then_inc(sem("scores_done"), 1)

            def stage(g, s):
                if s == 0:
                    pe.wait_ge(sem("z_out_act"), 5 * g + 1)
                    pe.wait_ge(sem("states_ready"), 4 * g)
                    pe.wait_ge(sem("level_taken"), (NL + 1) * g)
                    tr(SC[0][0:META, 0:P], vv[:, 0:META])
                    for c in range(NT):
                        last = tr(HB[0][:, c * P:(c + 1) * P], vv[:, META + c * P:META + (c + 1) * P])
                    last.then_inc(sem("v_turned"), 1)
                if s == 1:
                    pe.wait_ge(sem("kd_ready"), g + 1)
                    pe.wait_ge(sem("r_ready"), g)
                    tr(HB[1][0:META, 0:P], kd[:, 0:META])
                    for c in range(1, NT):
                        last = tr(HB[1][:, c * P:(c + 1) * P], kd[:, META + (c - 1) * P:META + c * P])
                    last.then_inc(sem("k_turned"), 1)
                    for c in range(NT):
                        last = mm(SC[1][:, c * P:(c + 1) * P], lhsT=kk[:, META + c * P:META + (c + 1) * P],
                                  rhs=qq[:, c * P:(c + 1) * P], start=True, stop=True)
                    last.then_inc(sem("scores_done"), 1)
                if s == 2:
                    pe.wait_ge(sem("kt_ready"), g + 1)
                    mm(HB[0][:, 0:P], lhsT=kt[0:META, 0, :], rhs=vt[0:META, 0, :], start=True, stop=True)
                    for c in range(1, NT):
                        last = mm(HB[0][:, c * P:(c + 1) * P], lhsT=kt[:, c, :], rhs=vt[:, c, :],
                                  start=True, stop=True)
                    last.then_inc(sem("updates_done"), 1)
                    pe.wait_ge(sem("kq_ready"), g + 1)
                    for n in range(4):
                        if n == 2:
                            pe.wait_ge(sem("level_taken"), (NL + 1) * g + 1)
                        scores(g, n, n // 2, n % 2 == 1)
                if s == 3:
                    pe.wait_ge(sem("level_taken"), (NL + 1) * g + 3)
                    scores(g, 4, 0, False)
                    scores(g, 5, 0, True)
                    pe.wait_ge(sem("level_taken"), (NL + 1) * g + 5)
                    scores(g, 6, 1, True)
                if s == 5:
                    pe.wait_ge(sem("states_ready"), 4 * g + 4)
                    pe.wait_ge(sem("level_taken"), (NL + 1) * g + 8)
                    for c in range(NT):
                        o = HB[1][:, c * P:(c + 1) * P]
                        mm(o, lhsT=S[:, c, :], rhs=qb[:, c * P:(c + 1) * P], start=True, stop=False)
                        last = mm(o, lhsT=vt[:, 1 + c, :], rhs=ST[:, c, :], start=False, stop=True)
                    last.then_inc(sem("o_done"), 1)
                if s == 6:
                    pe.wait_ge(sem("sqo_ready"), g + 1)
                    for c in range(NT):
                        last = mm(SC[1][:, c:c + 1], lhsT=rs[:, c * P:(c + 1) * P], rhs=ones_h[:, 0:1],
                                  start=True, stop=True)
                    last.then_inc(sem("norm_done"), 1)
                if s == 7:
                    pe.wait_ge(sem("rs_ready"), 2 * g + 2)
                    mm(SC[1], lhsT=ones[:], rhs=rs[:], start=True, stop=True).then_inc(sem("norm_done"), 1)

            pe.wait_ge(sem("u_lo_ready"), NT + 1)
            for u in range(NU):
                z_unit(0, u)
            with pe.Fori(1, HEADS) as h:
                stage(h - 1, 0)
                for u in range(NU):
                    z_unit(h, u)
                    if 0 < u + 1 < 4:
                        stage(h - 1, u + 1)
                    if u in (5, 6, 7):
                        stage(h - 1, u)

            def output_tile(n, j, hi, lo, ks):
                if 0 in ks:
                    pe.wait_ge(sem("mixer_lo"), MIX_U + n * KD + j + 1)
                    if n == 0 and j < 4:
                        pe.wait_ge(sem("z_out_act"), 5 * HEADS)
                        pe.wait_ge(sem("z_out_dve"), 3 * HEADS)
                    elif n == 0:
                        pe.wait_ge(sem("rnn_mixed"), j - 3)
                    elif j < 4:
                        pe.wait_ge(sem("rnn_mixed"), j + 5)
                    else:
                        pe.wait_ge(sem("conv_gated"), j - 3)
                for k in ks:
                    if n == 0 and j == 0:
                        pe.wait_ge(sem("r_lo_ready"), k + 1)
                    for w, t in ((wm_hi, hi), (wm_hi, lo), (wm_lo, hi)):
                        last = mm(ps[:, j % 4, :], lhsT=w[j % MW][:, k, :], rhs=t[:, k * SEQ:(k + 1) * SEQ],
                                  start=k == 0 and w is wm_hi and t is hi, stop=k == KD - 1 and w is wm_lo)
                if KD - 1 in ks:
                    last.then_inc(sem("unit_done"), 1)

            before, all_k = range(KD - 1), range(KD)
            stage(HEADS - 1, 0)
            stage(HEADS - 1, 1)
            output_tile(0, 0, r_hi, r_lo, before)
            stage(HEADS - 1, 2)
            output_tile(0, 1, r_hi, r_lo, before)
            stage(HEADS - 1, 3)
            output_tile(0, 2, r_hi, r_lo, before)
            stage(HEADS - 1, 5)
            stage(HEADS - 1, 6)
            output_tile(0, 3, r_hi, r_lo, before)
            stage(HEADS - 1, 7)
            for j in range(4):
                output_tile(0, j, r_hi, r_lo, [KD - 1])
            pe.wait_ge(sem("conv_step"), STEPS * HEADS)
            pe.wait_ge(sem("r_ready"), HEADS)
            for k in range(KD):
                last = mm(HB[0], lhsT=ones_d[:], rhs=conv[:, k * SEQ:(k + 1) * SEQ],
                          start=k == 0, stop=k == KD - 1)
            last.then_inc(sem("mean_done"), 1)
            for j in range(4, KD):
                output_tile(0, j, r_hi, r_lo, all_k)
                if j == 5:
                    for c in range(2):
                        pe.wait_ge(sem("ln_squared"), c + 1)
                        for k in range(4 * c, 4 * c + 4):
                            last = mm(HB[1], lhsT=ones_d[:], rhs=sq_ln[:, k, :], start=k == 0, stop=k == KD - 1)
                    last.then_inc(sem("var_done"), 1)
            beside = 5
            for k in range(beside):
                pe.wait_ge(sem("act_lo_ready"), k + 1)
                for j in range(4):
                    output_tile(1, j, act_hi, act_lo, [k])
            pe.wait_ge(sem("act_lo_ready"), KD)
            for j in range(4):
                output_tile(1, j, act_hi, act_lo, range(beside, KD))
            for j in range(4, KD):
                output_tile(1, j, act_hi, act_lo, all_k)

            def h_half(i, j, ks=range(KD)):
                if i >= 2:
                    pe.wait_ge(sem("h_ready"), 2 * i - 2)
                pe.wait_ge(sem("wo_lo_ready"), j + 1)
                for k in ks:
                    if i == 0:
                        pe.wait_ge(sem("mixed_lo_ready"), k + 1)
                    tok = slice(k * SEQ + i * P, k * SEQ + (i + 1) * P)
                    o = ps[:, 2 * (i % 2) + j, :]
                    mm(o, lhsT=mixed_hi[:, tok], rhs=wo_hi[j][:, k, :], start=k == 0, stop=False)
                    mm(o, lhsT=mixed_hi[:, tok], rhs=wo_lo[j][:, k, :], start=False, stop=False)
                    last = mm(o, lhsT=mixed_lo[:, tok], rhs=wo_hi[j][:, k, :], start=False, stop=k == KD - 1)
                if KD - 1 in ks:
                    last.then_inc(sem("wo_done"), 1)

            def turn_u2(i):
                pe.wait_ge(sem("u2_ready"), i + 1)
                pe.wait_ge(sem("u2t_ready"), i)
                for k in range(KD):
                    last = tr(ps[:, 4 + k // 4, (k % 4) * P:(k % 4 + 1) * P], u2[:, i, k * P:(k + 1) * P])
                last.then_inc(sem("u2_turned"), 1)

            def route_logits(i):
                pe.wait_ge(sem("u2t_ready"), i + 1)
                pe.wait_ge(sem("consts_landed"), 48)
                if i >= 2:
                    pe.wait_ge(sem("ranks_out"), i - 1)
                for k in range(KD):
                    last = mm(ps[:, 6 + i % 2, 0:E], lhsT=u2t[:, i % 2, k, :], rhs=wr[:, k, :],
                              start=k == 0, stop=k == KD - 1)
                last.then_inc(sem("logits_done"), 1)

            def route_ranks(i):
                pe.wait_ge(sem("members_ready"), i + 1)
                for j in range(i + 1):
                    last = mm(ps[:, 6 + i % 2, E:2 * E], lhsT=(tri if j == i else ones)[:],
                              rhs=member[:, j, :], start=j == 0, stop=j == i)
                if i == NT - 1:
                    for j in range(NT):
                        last = mm(ps[:, 6 + i % 2, 2 * E:3 * E], lhsT=ones[:], rhs=member[:, j, :],
                                  start=j == 0, stop=j == NT - 1)
                last.then_inc(sem("ranks_done"), 1)

            pe.wait_ge(sem("conv_gated"), KD)
            h_half(0, 0)
            h_half(0, 1)
            h_half(1, 0)
            turn_u2(0)
            h_half(1, 1)
            route_logits(0)
            for i in range(2, NT):
                h_half(i, 0)
                route_ranks(i - 2)
                turn_u2(i - 1)
                h_half(i, 1, range(0, KD // 2))
                route_logits(i - 1)
                h_half(i, 1, range(KD // 2, KD))
            route_ranks(NT - 2)
            turn_u2(NT - 1)
            route_logits(NT - 1)
            route_ranks(NT - 1)

            def table(r):
                pe.wait_ge(sem("slots_ready"), r + 1)
                for e in range(E):
                    for i in range(NT):
                        last = mm(ps[:, 7, e:e + 1], lhsT=slot_ohs[i][:, e, :], rhs=aval[:, i, e:e + 1],
                                  start=i == 0, stop=i == NT - 1)
                last.then_inc(sem("table_done"), 1)

            def turn_x(n):
                pe.wait_ge(sem("gathered"), 16 * (n + 1))
                for k in range(KD):
                    last = tr(ps[:, 6 + k // 4, (k % 4) * P:(k % 4 + 1) * P], xe[:, k * P:(k + 1) * P])
                last.then_inc(sem("x_turned"), 1)

            def three(out, k, s, c0, hi, lo, stop):
                w = slice(c0, c0 + 512)
                mm(out, lhsT=hi[:, k, :], rhs=w_hi[:, s % SPL, w], start=False, stop=False)
                mm(out, lhsT=hi[:, k, :], rhs=w_lo[s % RAW][:, w], start=False, stop=False)
                return mm(out, lhsT=lo[:, k, :], rhs=w_hi[:, s % SPL, w], start=False, stop=stop)

            def gate_up(n, unit0, s0, hidden_before=None):
                pe.wait_ge(sem("selg_ready"), n + 1)
                pe.wait_ge(sem("xlo_ready"), n + 1)
                for j in range(4):
                    if j % 2 == 0:
                        pe.wait_ge(sem("gate_out" if j == 0 else "up_out"), n)
                    mm(ps[:, j, :], lhsT=sel_g[0:64, :], rhs=b_hl[0:64, j * 512:(j + 1) * 512],
                       start=True, stop=False)
                for u in range(GU_U):
                    pe.wait_ge(sem("lo_done"), unit0 + u + 1)
                    for j in range(4):
                        last = three(ps[:, j, :], u, s0 + u, j * 512, xt_hi, xt_lo, u == GU_U - 1)
                    last.then_inc(sem("unit_used"), 1)
                    if u == 1 and hidden_before is not None:
                        turn_h(hidden_before)

            def down(n, unit0, s0):
                pe.wait_ge(sem("seld_ready"), n + 1)
                pe.wait_ge(sem("hlo_ready"), n + 1)
                pe.wait_ge(sem("y_ready"), n)
                for j in range(2):
                    mm(ps[:, 4 + j, :], lhsT=sel_d[0:64, :], rhs=b_hl[0:64, (4 + j) * 512:(5 + j) * 512],
                       start=True, stop=False)
                for v in range(DN_U):
                    pe.wait_ge(sem("lo_done"), unit0 + v + 1)
                    for k in range(2):
                        for j in range(2):
                            last = three(ps[:, 4 + j, :], 2 * v + k, s0 + v,
                                         k * D + j * 512, ht_hi, ht_lo, v == DN_U - 1 and k == 1)
                    last.then_inc(sem("unit_used"), 1)

            def turn_h(n):
                pe.wait_ge(sem("h_act_ready"), n + 1)
                pe.wait_ge(sem("xlo_ready"), n + 2)
                for k in range(KD):
                    last = tr(ps[:, 6 + k // 4, (k % 4) * P:(k % 4 + 1) * P], u_act[:, k * P:(k + 1) * P])
                last.then_inc(sem("h_turned"), 1)

            def experts(r):
                base = r * E
                unit = r * PASS_U
                table(r)
                pe.wait_ge(sem("table_ready"), r + 1)
                turn_x(base)
                gate_up(base, unit, 0)
                turn_x(base + 1)
                with pe.Fori(1, E - 1) as e:
                    gate_up(base + e, unit - DN_U + e * STEP_U, GU_U, base + e - 1)
                    pe.wait_ge(sem("hlo_ready"), base + e)
                    turn_x(base + e + 1)
                    down(base + e - 1, unit - DN_U + e * STEP_U + GU_U, GU_U + GU_U)
                e = E - 1
                gate_up(base + e, unit - DN_U + e * STEP_U, GU_U, base + e - 1)
                down(base + e - 1, unit - DN_U + e * STEP_U + GU_U, GU_U + GU_U)
                turn_h_last(base + e)
                down(base + e, unit - DN_U + E * STEP_U, GU_U)

            def turn_h_last(n):
                pe.wait_ge(sem("h_act_ready"), n + 1)
                for k in range(KD):
                    last = tr(ps[:, 6 + k // 4, (k % 4) * P:(k % 4 + 1) * P], u_act[:, k * P:(k + 1) * P])
                last.then_inc(sem("h_turned"), 1)

            experts(0)
            more_passes(pe, experts)
            pe.wait_ge(sem("gate_diag"), 1)
            for i in range(NT):
                pe.wait_ge(y4_landed[i][0], 16)
                if i >= 2:
                    pe.wait_ge(sem("combine_step"), 2 * (i - 2) + 1)
                for k in range(2):
                    for j in range(2):
                        last = mm(ps[:, 2 * (i % 2) + j, :], lhsT=gate_diag[:, i, k, :],
                                  rhs=y4[i][:, k, j * 512:(j + 1) * 512], start=k == 0, stop=k == 1)
                last.then_inc(sem("two_combined"), 1)

        @block.scalar
        def _(act):
            A = act.activation
            def root(n, i):
                A(rstd[0:n, i:i + 1], ss[0:n, i:i + 1], ACT.Sqrt, bias=eps_rms[0:n, :]).then_inc(sem("x_root"), 1)

            act.wait_ge(sem("c_ones"), 4)
            for i in range(NT + 1):
                src, n = (x_sb[:, i, :], P) if i < NT else (m_sb[0:META, :], META)
                act.wait_ge(x_landed[i], 16)
                if i > 0:
                    act.wait_ge(sem("ss_ready"), i)
                A(junk[0:n, :], src, ACT.Square, scale=D ** -0.5, accum_out=ss[0:n, i:i + 1]).then_inc(sem("ss_ready"), 1)
                act.wait_ge(sem("ss_ready"), i + 1)
                root(n, i)

            def both(t):
                return t.rearrange("p (c n) -> p c n", c=2)

            def z_act(h, u):
                act.wait_ge(sem("unit_done"), NU * h + u + 1)
                pair, bank = Z[u % 2][:, :, 0:HALF], Z[u % 2][:, 0, :]
                if UNITS[u] == G_F:
                    A(both(sf[:]), pair, ACT.Sigmoid).then_inc(sem("z_out_act"), 1)
                if UNITS[u] == G_I:
                    A(both(vv[:]), pair, ACT.Copy).then_inc(sem("z_out_act"), 1)
                if UNITS[u] == G_Q:
                    A(tq[:], bank, ACT.Sigmoid).then_inc(sem("sig_ready"), 1)
                if UNITS[u] == G_CG:
                    A(both(tc[:]), pair, ACT.Sigmoid).then_inc(sem("z_out_act"), 1)
                if UNITS[u] == G_GA:
                    A(cols(sg_a, h), bank, ACT.Sigmoid).then_inc(sem("z_out_act"), 1)
                if UNITS[u] == G_GB:
                    A(cols(sg_b, h), bank, ACT.Sigmoid).then_inc(sem("z_out_act"), 1)
                if UNITS[u] == G_OG:
                    A(tg[:], bank, ACT.Sigmoid).then_inc(sem("sig_ready"), 1)

            def log_f(h):
                act.wait_ge(sem("lb"), 5)
                act.wait_ge(sem("z_out_act"), 5 * h + 2)
                A(lf[:], sf[:], ACT.Ln, bias=lb[:, ds(h, 1)], scale=omlb[:, ds(h, 1)]).then_inc(sem("lf_ready"), 1)

            def exps(g):
                act.wait_ge(sem("ke_diff"), g + 1)
                A(ke[:], ke[:], ACT.Exp)
                A(eb[:], bb[:, META:TOK], ACT.Exp).then_inc(sem("ek_ready"), 1)

            def level_exps(g):
                act.wait_ge(sem("level_diff"), g + 1)
                A(D_l[:], D_l[:], ACT.Exp).then_inc(sem("el_ready"), 1)

            def vt_out(g):
                act.wait_ge(sem("v_turned"), g + 1)
                A(vt[0:META, 0, :], SC[0][0:META, 0:P], ACT.Copy)
                A(vt[:, 1:5, :], HB[0].rearrange("p (c n) -> p c n", c=4), ACT.Copy).then_inc(sem("vt_ready"), 1)

            def kt_out(g):
                act.wait_ge(sem("k_turned"), g + 1)
                A(kt[0:META, 0, :], HB[1][0:META, 0:P], ACT.Copy)
                A(kt[:, 1:4, :], HB[1][:, P:].rearrange("p (c n) -> p c n", c=3), ACT.Copy).then_inc(sem("kt_ready"), 1)

            def root_o(g):
                act.wait_ge(sem("norm_done"), 2 * g + 1)
                A(o_rstd[:], SC[1][:, 0:NT], ACT.Sqrt, bias=eps_rms[:]).then_inc(sem("rs_root"), 1)

            def square_o(g):
                act.wait_ge(sem("o_done"), g + 1)
                A(rs[:], HB[1], ACT.Square).then_inc(sem("sqo_ready"), 1)

            def unit(h, u):
                if UNITS[u] != G_CV:
                    z_act(h, u)
                weights_hi(h, u)

            def weights_hi(h, u):
                act.wait_ge(w_landed[u % MW], 16 * (2 * h + (u + MW) // MW + 1))
                act.wait_ge(sem("unit_done"), h * NU + u + 1)
                A(wm_hi[u % MW][:], wm[u % MW][:], ACT.Copy).then_inc(sem("mixer_hi"), 1)

            def split_hi_of(dst, src, ready, k, signal):
                act.wait_ge(sem(ready), k + 1)
                A(cols(dst, k), cols(src, k), ACT.Copy).then_inc(sem(signal), 1)

            for i in range(NT + 1):
                t = slice(META + i * P, META + (i + 1) * P) if i < NT else slice(0, META)
                act.wait_ge(sem("u_ready"), i + 1)
                A(u_hi[:, :, t], u_fm[:, :, t], ACT.Copy).then_inc(sem("u_hi_ready"), 1)
            act.wait_ge(sem("lb_shifted"), 1)
            A(lbw[:, :, 2:4], lbw[:, :, 0:2], ACT.Exp).then_inc(sem("lb_exp"), 1)
            for k in range(MW):
                act.wait_ge(w_landed[k], 16)
                A(wm_hi[k][:], wm[k][:], ACT.Copy).then_inc(sem("mixer_hi"), 1)
            for u in range(NU - 1):
                unit(0, u)
                if u == 3:
                    log_f(0)
            z_act(0, NU - 1)
            exps(0)
            with act.Fori(1, HEADS) as h:
                level_exps(h - 1)
                vt_out(h - 1)
                weights_hi(h - 1, 7)
                unit(h, 0)
                kt_out(h - 1)
                for u in range(1, 6):
                    unit(h, u)
                    if u == 3:
                        log_f(h)
                square_o(h - 1)
                z_act(h, 6)
                root_o(h - 1)
                weights_hi(h, 6)
                z_act(h, 7)
                exps(h)
            vt_out(HEADS - 1)
            for k in range(KD - 1):
                split_hi_of(r_hi, r_fm, "r_ready", k, "r_hi_ready")
            level_exps(HEADS - 1)
            weights_hi(HEADS - 1, 7)
            kt_out(HEADS - 1)
            square_o(HEADS - 1)
            root_o(HEADS - 1)
            split_hi_of(r_hi, r_fm, "r_ready", KD - 1, "r_hi_ready")

            def last_weights(j, n):
                done = MIX_U + n * KD + j
                act.wait_ge(w_landed[j % MW], 16 * ((done + MW) // MW + 1))
                act.wait_ge(sem("unit_done"), done + 1)
                A(wm_hi[j % MW][:], wm[j % MW][:], ACT.Copy).then_inc(sem("mixer_hi"), 1)

            def wo_high(j):
                act.wait_ge(sem(f"wo_landed{j}"), 16)
                A(wo_hi[j][:], wo[j][:], ACT.Copy).then_inc(sem("wo_hi_ready"), 1)

            for j in range(4):
                last_weights(j, 0)
            for c in range(2):
                act.wait_ge(sem("centred"), c + 1)
                A(sq_ln[:, 4 * c:4 * c + 4, :], conv[:, 4 * c * SEQ:(4 * c + 4) * SEQ].rearrange(
                    "p (k n) -> p k n", k=4), ACT.Square).then_inc(sem("ln_squared"), 1)
            wo_high(0)
            last_weights(4, 0)
            act.wait_ge(sem("var_done"), 1)
            A(rstd_ln[:], HB[1], ACT.Sqrt, bias=eps_ln[:]).then_inc(sem("ln_root"), 1)
            last_weights(5, 0)
            for k in range(KD):
                act.wait_ge(sem("scaled"), k + 1)
                if k >= 2:
                    act.wait_ge(sem("act_ready"), k - 1)
                A(ysig[:, k % 2, :], conv[:, k * SEQ:(k + 1) * SEQ], ACT.Sigmoid,
                  bias=PT[:, R_LNB * KD + k:R_LNB * KD + k + 1]).then_inc(sem("ln_sigmoid"), 1)
                if k >= 1:
                    split_hi_of(act_hi, conv, "act_ready", k - 1, "act_hi_ready")
                if k in (1, 3):
                    last_weights(6 + k // 2, 0)
            split_hi_of(act_hi, conv, "act_ready", KD - 1, "act_hi_ready")
            for j in range(KD):
                if j < KD - MW:
                    last_weights(j, 1)
                if j == 5:
                    wo_high(1)
                if j >= 1:
                    split_hi_of(mixed_hi, sg_b, "mixed", j - 1, "mixed_hi_ready")
            split_hi_of(mixed_hi, sg_b, "mixed", KD - 1, "mixed_hi_ready")
            for i in range(NT):
                act.wait_ge(sem("h_ready"), 2 * (i + 1))
                A(u2[:, i, :], h_sb[:, i, :], ACT.Square, scale=D ** -0.5,
                  accum_out=ss[:, i:i + 1]).then_inc(sem("rows_squared"), 1)
                act.wait_ge(sem("rows_squared"), i + 1)
                A(rstd[:, i:i + 1], ss[:, i:i + 1], ACT.Sqrt, bias=eps_rms[:]).then_inc(sem("rows_root"), 1)
            act.wait_ge(sem("bias_landed"), 64)
            A(b_hl[0:64, :], b_raw[0:64, :], ACT.Copy).then_inc(sem("bias_hi"), 1)
            act.wait_ge(sem("gate_shifted"), 1)
            A(gex[:], gex[:], ACT.Exp).then_inc(sem("gate_exp"), 1)
            def split_hi(landed, n, s, first=False):
                act.wait_ge(raw_landed[s % RAW], landed)
                if not first:
                    act.wait_ge(sem("unit_used"), n - SPL + 1)
                A(w_hi[:, s % SPL, :], raw[s % RAW][:], ACT.Copy).then_inc(sem("hi_done"), 1)

            def xt_hi_out(n):
                act.wait_ge(sem("x_turned"), n + 1)
                A(xt_hi[:], ps[:, 6:8, :].rearrange("p a (b c) -> p (a b) c", b=4), ACT.Copy).then_inc(sem("xhi_ready"), 1)

            def ht_hi_out(n):
                act.wait_ge(sem("h_turned"), n + 1)
                A(ht_hi[:], ps[:, 6:8, :].rearrange("p a (b c) -> p (a b) c", b=4), ACT.Copy).then_inc(sem("hhi_ready"), 1)

            def gate_sigmoid(n):
                act.wait_ge(sem("gate_out"), n + 1)
                A(g_sig[:], g_act[:], ACT.Sigmoid, scale=ALPHA).then_inc(sem("gate_sigmoid"), 1)

            def y_out(n, unit_end):
                act.wait_ge(sem("unit_used"), unit_end)
                act.wait_ge(sem("scattered"), 16 * n)
                A(y_sb[:].rearrange("p (a c) -> p a c", a=2), ps[:, 4:6, :], ACT.Copy).then_inc(sem("y_ready"), 1)

            def experts_act(r):
                base, unit = r * E, r * PASS_U
                turns = r * (PASS_U // RAW)

                def peeled(q):
                    split_hi(16 * (turns + q // RAW + 1), unit + q, q, first=isinstance(r, int) and q < SPL)

                for q in range(2):
                    peeled(q)
                xt_hi_out(base)
                for q in range(2, GU_U + SPL - 1):
                    peeled(q)
                xt_hi_out(base + 1)
                gate_sigmoid(base)
                peeled(GU_U + SPL - 1)
                with act.Fori(1, E - 1) as e:
                    first = unit - DN_U + e * STEP_U

                    def split(u):
                        split_hi(16 * (turns + e - 1 + (GU_U + u) // RAW + 1), first + u, GU_U + u)

                    for u in range(SPL, SPL + 2):
                        split(u)
                    ht_hi_out(base + e - 1)
                    for u in range(SPL + 2, GU_U + SPL - 1):
                        split(u)
                    gate_sigmoid(base + e)
                    xt_hi_out(base + e + 1)
                    for u in range(GU_U + SPL - 1, STEP_U + SPL):
                        split(u)
                    y_out(base + e - 1, first + STEP_U)
                first = PASS_U - DN_U - STEP_U
                for u in range(SPL, SPL + 2):
                    peeled(first + u)
                ht_hi_out(base + E - 2)
                for u in range(SPL + 2, GU_U + SPL - 1):
                    peeled(first + u)
                gate_sigmoid(base + E - 1)
                for u in range(GU_U + SPL - 1, STEP_U + SPL - 2):
                    peeled(first + u)
                y_out(base + E - 2, unit + PASS_U - DN_U)
                ht_hi_out(base + E - 1)
                for u in range(STEP_U + SPL - 2, STEP_U + SPL):
                    peeled(first + u)
                y_out(base + E - 1, unit + PASS_U)

            act.wait_ge(sem("u2_kept"), 1)
            experts_act(0)
            more_passes(act, experts_act)
            for i in range(NT):
                act.wait_ge(sem("combined"), i + 1)
                if i > 0:
                    act.wait_ge(sem("rows_squared"), NT + i)
                A(junk3[:], fin[:, i, :], ACT.Square, scale=D ** -0.5,
                  accum_out=ss[:, i:i + 1]).then_inc(sem("rows_squared"), 1)
                act.wait_ge(sem("rows_squared"), NT + i + 1)
                A(rstd[:, i:i + 1], ss[:, i:i + 1], ACT.Sqrt, bias=eps_rms[:]).then_inc(sem("rows_root"), 1)

        @block.vector
        def _(dve):
            TT, TS, STT = dve.tensor_tensor, dve.tensor_scalar, dve.scalar_tensor_tensor

            def par(row, h):
                return PT[:, ds(row * KD + h, 1)]

            def both(t):
                return t.rearrange("p (c n) -> p c n", c=2)

            dve.wait_ge(sem("rows_turned"), 1)
            dve.tensor_copy(PT[:].rearrange("p (r k) -> p k r", k=KD),
                            ps[:, 7, 0:KD * NP_ROWS].rearrange("p (k r) -> p k r", k=KD)).then_inc(sem("params_ready"), 1)
            dve.wait_ge(sem("params_ready"), 1)
            l0, l1 = PT[:, R_LB * KD:R_LB * KD + KD], PT[:, (R_LB + 1) * KD:(R_LB + 2) * KD]
            TT(lbw[:, :, 2], l0, l1, ALU.max).then_inc(sem("lb"), 1)
            dve.wait_ge(sem("lb"), 1)
            TT(lbw[:, :, 0], l0, lbw[:, :, 2], ALU.subtract)
            TT(lbw[:, :, 1], l1, lbw[:, :, 2], ALU.subtract).then_inc(sem("lb_shifted"), 1)

            def normed(i):
                t, n = (x_sb[:, i, :], P) if i < NT else (m_sb[0:META, :], META)
                dve.wait_ge(sem("x_root"), i + 1)
                dve.reciprocal(rstd[0:n, i:i + 1], rstd[0:n, i:i + 1]).then_inc(sem("x_rstd"), 1)
                dve.wait_ge(sem("x_rstd"), i + 1)
                TS(t, t, rstd[0:n, i:i + 1], None, ALU.mult).then_inc(sem("x_normed"), 1)

            def turned(i):
                n, t = (P, slice(META + i * P, META + (i + 1) * P)) if i < NT else (META, slice(0, META))
                src = (ps[:, 2 * (i % 2):2 * (i % 2) + 2, :].rearrange("p a (b c) -> p (a b) c", b=4) if i < NT else
                       ps[:, 4, 0:KD * META].rearrange("p (k n) -> p k n", k=KD))
                dve.wait_ge(sem("x_t"), i + 1)
                TT(u_fm[:, :, t], src, PT[:, R_GMIX * KD:(R_GMIX + 1) * KD].unsqueeze(2).to_broadcast([P, KD, n]),
                   ALU.mult).then_inc(sem("u_ready"), 1)

            def u_low(i):
                t = slice(META + i * P, META + (i + 1) * P) if i < NT else slice(0, META)
                dve.wait_ge(sem("u_hi_ready"), i + 1)
                TT(u_lo[:, :, t], u_fm[:, :, t], u_hi[:, :, t].bitcast(F32), ALU.subtract).then_inc(sem("u_lo_ready"), 1)

            normed(0)
            for i in range(NT + 1):
                if i < NT:
                    normed(i + 1)
                turned(i)
                if i > 0:
                    u_low(i - 1)
            u_low(NT)
            dve.wait_ge(sem("lb_exp"), 1)
            TT(lbw[:, :, 0], lbw[:, :, 2], lbw[:, :, 3], ALU.add).then_inc(sem("lb"), 1)
            dve.wait_ge(sem("lb"), 2)
            dve.reciprocal(lbw[:, :, 1], lbw[:, :, 0]).then_inc(sem("lb"), 1)
            dve.wait_ge(sem("lb"), 3)
            TT(lb[:], lbw[:, :, 2], lbw[:, :, 1], ALU.mult)
            TT(omlb[:], lbw[:, :, 3], lbw[:, :, 1], ALU.mult).then_inc(sem("lb"), 1)
            dve.wait_ge(sem("lb"), 4)
            TS(neg_omlb[:], omlb[:], -1.0, None, ALU.mult).then_inc(sem("lb"), 1)

            def z_dve(h, u):
                dve.wait_ge(sem("unit_done"), NU * h + u + 1)
                if UNITS[u] == G_Q:
                    dve.wait_ge(sem("sig_ready"), 2 * h + 1)
                    TT(qq[:], Z[u % 2][:, 0, :], tq[:], ALU.mult).then_inc(sem("z_out_dve"), 1)
                if UNITS[u] == G_CV:
                    dve.wait_ge(sem("z_out_act"), 5 * h + 3)
                    dve.wait_ge(sem("conv_step"), STEPS * h)
                    TT(both(ap_[:, PADL:]), Z[u % 2][:, :, 0:HALF], both(tc[:]), ALU.mult).then_inc(sem("z_out_dve"), 1)
                if UNITS[u] == G_OG:
                    dve.wait_ge(sem("sig_ready"), 2 * h + 2)
                    dve.wait_ge(sem("r_ready"), h)
                    TT(gg[:], Z[u % 2][:, 0, :], tg[:], ALU.mult).then_inc(sem("z_out_dve"), 1)

            def decays(g):
                dve.wait_ge(sem("lf_ready"), g + 1)
                TS(kk[:], sf[:], neg_omlb[:, ds(g, 1)], omlb[:, ds(g, 1)], ALU.mult, ALU.add)
                dve.tensor_tensor_scan(bb[:], keep[:], lf[:], 0.0, ALU.mult, ALU.add).then_inc(sem("b_ready"), 1)
                dve.wait_ge(sem("b_ready"), g + 1)
                TT(ke[:, 0:META], bb[:, META - 1:META].to_broadcast([P, META]), bb[:, 0:META], ALU.subtract)
                chunks = bb[:, META:META + 3 * P].rearrange("p (c n) -> p c n", c=3)
                TT(ke[:, META:].rearrange("p (c n) -> p c n", c=3), chunks[:, :, P - 1:P].to_broadcast([P, 3, P]),
                   chunks, ALU.subtract).then_inc(sem("ke_diff"), 1)
                for n, m in enumerate(LEVELS):
                    b, d = lvl(bb[:, META:TOK], m), lvl(D_l[:, n, :], m)
                    ref = b[:, :, 0, m - 1:m].to_broadcast([P, SEQ // (2 * m), m])
                    TT(d[:, :, 0, :], ref, b[:, :, 0, :], ALU.subtract)
                    last = TT(d[:, :, 1, :], b[:, :, 1, :], ref, ALU.subtract)
                last.then_inc(sem("level_diff"), 1)

            def decayed(g):
                dve.wait_ge(sem("ek_ready"), g + 1)
                TT(kd[:], kk[:, 0:META + 3 * P], ke[:], ALU.mult).then_inc(sem("kd_ready"), 1)
                TT(qb[:], qq[:], eb[:], ALU.mult)

            def levels_decayed(g):
                dve.wait_ge(sem("el_ready"), g + 1)
                for n, m in enumerate(LEVELS):
                    d = lvl(D_l[:, n, :], m)
                    TT(d[:, :, 0, :], d[:, :, 0, :], lvl(kk[:, META:TOK], m)[:, :, 0, :], ALU.mult)
                    last = TT(d[:, :, 1, :], d[:, :, 1, :], lvl(qq[:], m)[:, :, 1, :], ALU.mult)
                last.then_inc(sem("kq_ready"), 1)

            def conv_taps(g, t0, t1):
                c = cols(conv, g)
                for t in range(t0, t1):
                    done = sem("conv_step")
                    if t == 0:
                        dve.wait_ge(sem("z_out_dve"), 3 * g + 2)
                        TS(c, ap_[:, 0:SEQ], par(0, g), par(R_BDW, g), ALU.mult, ALU.add).then_inc(done, 1)
                    elif t == 1:
                        TS(conv_odd[:], ap_[:, 1:1 + SEQ], par(1, g), None, ALU.mult).then_inc(done, 1)
                    elif t < TAPS:
                        dve.wait_ge(done, STEPS * g + t - 1)
                        o = conv_odd[:] if t % 2 else c
                        STT(o, ap_[:, t:t + SEQ], par(t, g), o, ALU.mult, ALU.add).then_inc(done, 1)
                    else:
                        dve.wait_ge(done, STEPS * g + TAPS)
                        TT(c, c, conv_odd[:], ALU.add).then_inc(done, 1)

            def take_scores(g, step, levels, bank):
                wait_alone(dve, sem("scores_done"), 5 * g + step)
                for n in levels:
                    wait_alone(dve, sem("level_taken"), (NL + 1) * g + n + 1)
                    m = LEVELS[n]
                    st = ST[:].rearrange("p c (b two m) -> p c b two m", two=2, m=m)[:, :, :, 1, :]
                    mask = masks[:, n, :].rearrange("p (b m) -> p b m", m=m).bitcast(U32)
                    dve.copy_predicated(
                        st, mask.unsqueeze(1).to_broadcast([P, NT, P // (2 * m), m]),
                        SC[bank][:, (n % 2) * 256:(n % 2 + 1) * 256].rearrange(
                            "p (c b m) -> p c b m", c=NT, m=m)).then_inc(sem("level_taken"), 1)

            def states(g):
                dve.wait_ge(sem("updates_done"), g + 1)
                dve.tensor_copy(S[:, 0, :], HB[0][:, 0:P]).then_inc(sem("states_ready"), 1)
                for c in range(1, NT):
                    dve.wait_ge(sem("states_ready"), 4 * g + c)
                    STT(S[:, c, :], S[:, c - 1, :], eb[:, c * P - 1:c * P], HB[0][:, c * P:(c + 1) * P],
                        ALU.mult, ALU.add).then_inc(sem("states_ready"), 1)

            def diagonal(g):
                wait_alone(dve, sem("scores_done"), 5 * g + 1)
                dve.copy_predicated(ST[:], ident[:].bitcast(U32).unsqueeze(1).to_broadcast([P, NT, P]),
                                    SC[1].rearrange("p (c n) -> p c n", c=NT)).then_inc(sem("level_taken"), 1)

            def norm_scale(g):
                dve.wait_ge(sem("rs_root"), g + 1)
                dve.reciprocal(o_rstd[:], o_rstd[:]).then_inc(sem("rs_ready"), 1)
                dve.wait_ge(sem("rs_ready"), 2 * g + 1)
                TT(rs[:].rearrange("p (c n) -> p c n", c=NT), ident[:].unsqueeze(1).to_broadcast([P, NT, P]),
                   o_rstd[:].unsqueeze(2).to_broadcast([P, NT, P]), ALU.mult).then_inc(sem("rs_ready"), 1)

            def finish(g):
                dve.wait_ge(sem("norm_done"), 2 * g + 2)
                TT(rs[:], SC[1], gg[:], ALU.mult).then_inc(sem("on_ready"), 1)
                dve.wait_ge(sem("on_ready"), g + 1)
                STT(cols(r_fm, g), HB[1], par(R_GON, g), rs[:], ALU.mult, ALU.mult).then_inc(sem("r_ready"), 1)

            def mixer_low(n, s):
                dve.wait_ge(sem("mixer_hi"), n + 1)
                TT(wm_lo[s % MW][:], wm[s % MW][:], wm_hi[s % MW][:].bitcast(F32),
                   ALU.subtract).then_inc(sem("mixer_lo"), 1)

            def low(dst, src, hi, ready, k, signal):
                dve.wait_ge(sem(ready), k + 1)
                TT(cols(dst, k), cols(src, k), cols(hi, k).bitcast(F32), ALU.subtract).then_inc(sem(signal), 1)

            def chunk_work(g, after_unit, fill):
                decayed(g)
                conv_taps(g, 0, 4)
                levels_decayed(g)
                mixer_low(g * NU + (NU - 1 + MW), NU - 1)
                diagonal(g)
                fill(0)
                conv_taps(g, 4, 8)
                fill(1)
                take_scores(g, 2, (0, 1), 0)
                take_scores(g, 3, (2, 3), 1)
                states(g)
                after_unit(2)
                conv_taps(g, 8, 15)
                fill(2)
                take_scores(g, 4, (4, 5), 0)
                take_scores(g, 5, (6,), 1)
                conv_taps(g, 15, STEPS)

            for n in range(MW):
                mixer_low(n, n)
            dve.wait_ge(sem("lb"), 5)
            dve.wait_ge(sem("c_mask"), 2 * NL)
            for u in range(NU):
                if u in (2, 4, 7):
                    z_dve(0, u)
                if u == 4:
                    decays(0)
                if u < NU - 1:
                    mixer_low(u + MW, u)
            with dve.Fori(1, HEADS) as h:
                chunk_work(h - 1, lambda u: z_dve(h, u), lambda u: mixer_low(h * NU + (u + MW), u))
                z_dve(h, 4)
                mixer_low(h * NU + (3 + MW), 3)
                mixer_low(h * NU + (4 + MW), 4)
                decays(h)
                mixer_low(h * NU + (5 + MW), 5)
                norm_scale(h - 1)
                mixer_low(h * NU + (6 + MW), 6)
                finish(h - 1)
                z_dve(h, 7)
            g = HEADS - 1
            decayed(g)
            for k in range(KD - 1):
                low(r_lo, r_fm, r_hi, "r_hi_ready", k, "r_lo_ready")
            levels_decayed(g)
            mixer_low(MIX_U + MW - 1, NU - 1)
            diagonal(g)
            conv_taps(g, 0, 6)
            take_scores(g, 2, (0, 1), 0)
            take_scores(g, 3, (2, 3), 1)
            states(g)
            conv_taps(g, 6, 12)
            take_scores(g, 4, (4, 5), 0)
            take_scores(g, 5, (6,), 1)
            conv_taps(g, 12, 20)
            norm_scale(g)
            conv_taps(g, 20, 22)
            finish(g)
            low(r_lo, r_fm, r_hi, "r_hi_ready", KD - 1, "r_lo_ready")
            conv_taps(g, 22, STEPS)

            def tiles(c):
                return conv[:, 4 * c * SEQ:(4 * c + 4) * SEQ].rearrange("p (k n) -> p k n", k=4)

            def wo_low(j):
                dve.wait_ge(sem("wo_hi_ready"), j + 1)
                TT(wo_lo[j][:], wo[j][:], wo_hi[j][:].bitcast(F32), ALU.subtract).then_inc(sem("wo_lo_ready"), 1)

            def rnn_out(j):
                dve.wait_ge(sem("unit_done"), MIX_U + j + 1)
                TT(cols(sg_b, j), ps[:, j % 4, :], cols(sg_b, j), ALU.mult).then_inc(sem("rnn_mixed"), 1)
                mixer_low(MIX_U + MW + j, j)

            for j in range(4):
                rnn_out(j)
            dve.wait_ge(sem("mean_done"), 1)
            for c in range(2):
                TT(tiles(c), tiles(c), HB[0].unsqueeze(1).to_broadcast([P, 4, SEQ]),
                   ALU.subtract).then_inc(sem("centred"), 1)

            rnn_out(4)
            wo_low(0)
            rnn_out(5)
            dve.wait_ge(sem("ln_root"), 1)
            dve.reciprocal(rstd_ln[:], rstd_ln[:]).then_inc(sem("ln_rstd"), 1)
            dve.wait_ge(sem("ln_rstd"), 1)
            dve.wait_ge(sem("centred"), 2)

            def scaled(k):
                STT(cols(conv, k), cols(conv, k), par(R_LNG, k), rstd_ln[:], ALU.mult, ALU.mult).then_inc(sem("scaled"), 1)

            scaled(0)
            for k in range(KD):
                if k < KD - 1:
                    scaled(k + 1)
                if k >= 1:
                    low(act_lo, conv, act_hi, "act_hi_ready", k - 1, "act_lo_ready")
                dve.wait_ge(sem("ln_sigmoid"), k + 1)
                STT(cols(conv, k), cols(conv, k), par(R_LNB, k), ysig[:, k % 2, :], ALU.add, ALU.mult).then_inc(sem("act_ready"), 1)
                if k in (0, 2):
                    rnn_out(6 + k // 2)
            low(act_lo, conv, act_hi, "act_hi_ready", KD - 1, "act_lo_ready")

            for j in range(KD):
                dve.wait_ge(sem("unit_done"), MIX_U + KD + j + 1)
                STT(aa[:, j % 2, :], ps[:, j % 4, :], par(R_BCO, j), cols(sg_a, j), ALU.add,
                    ALU.mult).then_inc(sem("conv_gated"), 1)
                dve.wait_ge(sem("conv_gated"), j + 1)
                TT(cols(sg_b, j), cols(sg_b, j), aa[:, j % 2, :], ALU.add).then_inc(sem("mixed"), 1)
                if j < KD - MW:
                    mixer_low(MIX_U + KD + MW + j, j)
                if j >= 1:
                    low(mixed_lo, sg_b, mixed_hi, "mixed_hi_ready", j - 1, "mixed_lo_ready")
                if j == 5:
                    wo_low(1)
            low(mixed_lo, sg_b, mixed_hi, "mixed_hi_ready", KD - 1, "mixed_lo_ready")
            dve.wait_ge(sem("h_landed"), 16)
            dve.wait_ge(sem("consts_landed"), 48)
            dve.wait_ge(sem("c_sel"), 3)
            step = [0]

            def link(ins):
                step[0] += 1
                ins.then_inc(sem("routing_step"), 1)
                dve.wait_ge(sem("routing_step"), step[0])

            def h_half(i, j):
                dve.wait_ge(sem("wo_done"), 2 * i + j + 1)
                c = slice(j * 512, (j + 1) * 512)
                TT(h_sb[:, i, c], h_sb[:, i, c], ps[:, 2 * (i % 2) + j, :], ALU.add).then_inc(sem("h_ready"), 1)

            def normed_rows(i):
                dve.wait_ge(sem("rows_root"), i + 1)
                dve.reciprocal(rstd[:, i:i + 1], rstd[:, i:i + 1]).then_inc(sem("rows_rstd"), 1)
                dve.wait_ge(sem("rows_rstd"), i + 1)
                STT(u2[:, i, :], h_sb[:, i, :], rstd[:, i:i + 1], gffn_bc[:], ALU.mult, ALU.mult).then_inc(sem("u2_ready"), 1)

            def turned_out(i):
                dve.wait_ge(sem("u2_turned"), i + 1)
                if i >= 2:
                    dve.wait_ge(sem("logits_done"), i - 1)
                dve.tensor_copy(u2t[:, i % 2], ps[:, 4:6, :].rearrange("p a (b c) -> p (a b) c", b=4)).then_inc(
                    sem("u2t_ready"), 1)

            def members(i):
                dve.wait_ge(sem("logits_done"), i + 1)
                link(TT(logits[:, i, :], ps[:, 6 + i % 2, 0:E], br_bc[:], ALU.add))
                link(dve.max(top_v[:, i, :], logits[:, i, :]))
                link(dve.max_index(top_i[:, i, :], top_v[:, i, :], logits[:, i, :]))
                link(dve.tensor_copy(top_f[:, i, :], top_i[:, i, 0:TOPK]))
                link(TT(oneh[:, i], iota_e[:].unsqueeze(1).to_broadcast([P, TOPK, E]),
                        top_f[:, i, :].unsqueeze(2).to_broadcast([P, TOPK, E]), ALU.is_equal))
                dve.reduce_sum(member[:, i, :], oneh[:, i].rearrange("p k e -> p e k"), AX_X).then_inc(
                    sem("members_ready"), 1)
                link(STT(choice[:, i, :], oneh[:, i, 2, :], 2.0, oneh[:, i, 1, :], ALU.mult, ALU.add))
                link(STT(choice[:, i, :], oneh[:, i, 3, :], 3.0, choice[:, i, :], ALU.mult, ALU.add))
                TT(aval[:, i, :], choice[:, i, :], tok1[:, i:i + 1].to_broadcast([P, E]), ALU.add)

            def slot_rows(i, part):
                e = slice(part * (E // 2), (part + 1) * (E // 2))
                return TT(slot_ohs[i][:, e, :], rankm[:, i, e].unsqueeze(2).to_broadcast([P, E // 2, P]),
                          iota_s[:].unsqueeze(1).to_broadcast([P, E // 2, P]), ALU.is_equal)

            def ranks(i):
                dve.wait_ge(sem("ranks_done"), i + 1)
                dve.wait_ge(sem("members_ready"), i + 1)
                STT(rankm[:, i, :], ps[:, 6 + i % 2, E:2 * E], 1.0, member[:, i, :],
                    ALU.add, ALU.mult).then_inc(sem("ranks_out"), 1)
                dve.wait_ge(sem("ranks_out"), i + 1)
                if i == NT - 1:
                    dve.reduce_max(cmax[:], ps[:, 6 + i % 2, 2 * E:3 * E], AX_X)
                link(TS(rankm[:, i, :], rankm[:, i, :], -1.0, None, ALU.add))

            h_half(0, 0)
            h_half(0, 1)
            normed_rows(0)
            turned_out(0)
            for i in range(1, NT):
                h_half(i, 0)
                h_half(i, 1)
                if i > 1:
                    slot_rows(i - 2, 1)
                normed_rows(i)
                if i == 1:
                    members(0)
                if i == NT - 1:
                    ranks(i - 1)
                turned_out(i)
                if i < NT - 1:
                    ranks(i - 1)
                slot_rows(i - 1, 0)
                members(i)
            slot_rows(NT - 2, 1)
            ranks(NT - 1)
            dve.tensor_copy(cmax_i[:], cmax[:]).then_inc(sem("count_ready"), 1)
            slot_rows(NT - 1, 0)
            slot_rows(NT - 1, 1).then_inc(sem("slots_ready"), 1)
            TT(gex[:], top_v[:, :, 0:TOPK], top_v[:, :, 0:1].to_broadcast([P, NT, TOPK]),
               ALU.subtract).then_inc(sem("gate_shifted"), 1)
            dve.wait_ge(sem("bias_hi"), 1)
            TT(b_hl[E:2 * E, :], b_raw[E:2 * E, :], b_hl[E:2 * E, :].bitcast(F32), ALU.subtract).then_inc(sem("bias_lo"), 1)
            dve.wait_ge(sem("gate_exp"), 1)
            link(dve.reduce_sum(gsum[:], gex[:], AX_X))
            link(dve.reciprocal(gsum[:], gsum[:]))
            link(TT(gates[:], gex[:], gsum[:].unsqueeze(2).to_broadcast([P, NT, TOPK]), ALU.mult))

            def table(r):
                if not isinstance(r, int):
                    for i in range(NT):
                        for part in range(2):
                            last = slot_rows(i, part)
                    last.then_inc(sem("slots_ready"), 1)
                dve.wait_ge(sem("table_done"), r + 1)
                TS(slot_eq[0:SLOTS, :], ps[0:SLOTS, 7, 0:E], 0.0, PAD, ALU.is_equal, ALU.mult).then_inc(sem("table_step"), 1)
                dve.wait_ge(sem("table_step"), 3 * r + 1)
                STT(slot_f[0:SLOTS, :], ps[0:SLOTS, 7, 0:E], -1.0, slot_eq[0:SLOTS, :], ALU.add, ALU.add).then_inc(sem("table_step"), 1)
                dve.wait_ge(sem("table_step"), 3 * r + 2)
                dve.tensor_copy(scat_i[0:SLOTS, :], slot_f[0:SLOTS, :]).then_inc(sem("table_step"), 1)
                dve.wait_ge(sem("table_step"), 3 * r + 3)
                TS(gath_i[0:SLOTS, :], scat_i[0:SLOTS, :], 2, None, ALU.logical_shift_right).then_inc(sem("table_ready"), 1)

            def select(buf, e, signal):
                dve.tensor_copy(buf[0:64, :], selbase[0:64, ds(e, 1)].to_broadcast([64, P])).then_inc(sem(signal), 1)

            def split_lo(n, s):
                dve.wait_ge(sem("hi_done"), n + 1)
                TT(w_lo[s % RAW][:], raw[s % RAW][:], w_hi[:, s % SPL, :].bitcast(F32),
                   ALU.subtract).then_inc(sem("lo_done"), 1)

            def low_of(dst, src, ready, turned, signal, n):
                dve.wait_ge(sem(turned), n + 1)
                dve.wait_ge(sem(ready), n + 1)
                TT(dst[:], ps[:, 6:8, :].rearrange("p a (b c) -> p (a b) c", b=4), src[:].bitcast(F32),
                   ALU.subtract).then_inc(sem(signal), 1)

            def xt_lo_out(n):
                low_of(xt_lo, xt_hi, "xhi_ready", "x_turned", "xlo_ready", n)

            def ht_lo_out(n):
                low_of(ht_lo, ht_hi, "hhi_ready", "h_turned", "hlo_ready", n)

            def gate_and_up(n, unit_end):
                dve.wait_ge(sem("unit_used"), unit_end)
                two = lambda t: t[:].rearrange("p (a c) -> p a c", a=2)
                TS(two(g_act), ps[:, 0:2, :], LIMIT, None, ALU.min).then_inc(sem("gate_out"), 1)
                TS(two(u_act), ps[:, 2:4, :], LIMIT, -LIMIT, ALU.min, ALU.max).then_inc(sem("up_out"), 1)

            def hidden(n):
                dve.wait_ge(sem("gate_sigmoid"), n + 1)
                dve.wait_ge(sem("up_out"), n + 1)
                TT(g_act[:], g_act[:], g_sig[:], ALU.mult).then_inc(sem("gate_silu"), 1)
                dve.wait_ge(sem("gate_silu"), n + 1)
                STT(u_act[:], u_act[:], 1.0, g_act[:], ALU.add, ALU.mult).then_inc(sem("h_act_ready"), 1)

            def experts_dve(r):
                base, unit = r * E, r * PASS_U
                if not isinstance(r, int):
                    dve.wait_ge(sem("scattered"), 16 * base)
                    TS(rankm[:], rankm[:], -float(SLOTS), None, ALU.add).then_inc(sem("rank_shift"), 1)
                    dve.wait_ge(sem("rank_shift"), r)
                table(r)
                select(sel_g, 0, "selg_ready")
                for q in range(2):
                    split_lo(unit + q, q)
                xt_lo_out(base)
                for q in range(2, SPL):
                    split_lo(unit + q, q)
                for q in range(SPL, GU_U + SPL - 1):
                    split_lo(unit + q, q)
                gate_and_up(base, unit + GU_U)
                select(sel_g, 1, "selg_ready")
                xt_lo_out(base + 1)
                hidden(base)
                split_lo(unit + GU_U + SPL - 1, GU_U + SPL - 1)
                with dve.Fori(1, E - 1) as e:
                    first = unit - DN_U + e * STEP_U
                    for u in range(SPL, SPL + 2):
                        split_lo(first + u, GU_U + u)
                    select(sel_d, e - 1, "seld_ready")
                    ht_lo_out(base + e - 1)
                    for u in range(SPL + 2, GU_U + SPL - 1):
                        split_lo(first + u, GU_U + u)
                    gate_and_up(base + e, first + GU_U)
                    hidden(base + e)
                    for u in range(GU_U + SPL - 1, GU_U + SPL + 1):
                        split_lo(first + u, GU_U + u)
                    select(sel_g, e + 1, "selg_ready")
                    xt_lo_out(base + e + 1)
                    for u in range(GU_U + SPL + 1, STEP_U + SPL):
                        split_lo(first + u, GU_U + u)
                first = PASS_U - DN_U - STEP_U
                for u in range(SPL, SPL + 2):
                    split_lo(unit + first + u, first + u)
                select(sel_d, E - 2, "seld_ready")
                ht_lo_out(base + E - 2)
                for u in range(SPL + 2, GU_U + SPL - 1):
                    split_lo(unit + first + u, first + u)
                gate_and_up(base + E - 1, unit + first + GU_U)
                hidden(base + E - 1)
                for u in range(GU_U + SPL - 1, STEP_U + SPL - 2):
                    split_lo(unit + first + u, first + u)
                dve.wait_ge(sem("h_turned"), base + E)
                select(sel_d, E - 1, "seld_ready")
                ht_lo_out(base + E - 1)
                for u in range(STEP_U + SPL - 2, STEP_U + SPL):
                    split_lo(unit + first + u, first + u)

            experts_dve(0)
            more_passes(dve, experts_dve)

            def scaled(i):
                dve.wait_ge(sem("rows_root"), NT + i + 1)
                dve.reciprocal(rstd[:, i:i + 1], rstd[:, i:i + 1]).then_inc(sem("rows_rstd"), 1)
                dve.wait_ge(sem("rows_rstd"), NT + i + 1)
                STT(fin[:, i, :], fin[:, i, :], rstd[:, i:i + 1], gfin_bc[:], ALU.mult, ALU.mult).then_inc(sem("final_ready"), 1)

            dve.wait_ge(sem("all_scattered"), 1)
            TT(gate_diag[:], ident[:].unsqueeze(1).unsqueeze(1).to_broadcast([P, NT, 2, P]),
               gates[:, :, 0:2].unsqueeze(3).to_broadcast([P, NT, 2, P]), ALU.mult).then_inc(sem("gate_diag"), 1)
            for i in range(NT):
                dve.wait_ge(sem("two_combined"), i + 1)
                two = lambda t: t[:, i, :].rearrange("p (a c) -> p a c", a=2)
                TT(two(fin), ps[:, 2 * (i % 2):2 * (i % 2) + 2, :], two(h_sb), ALU.add).then_inc(sem("combine_step"), 1)
                for k in range(2, TOPK):
                    dve.wait_ge(y4_landed[i][1], 16)
                    dve.wait_ge(sem("combine_step"), 2 * i + k - 1)
                    last = STT(fin[:, i, :], y4[i][:, k, :], gates[:, i, k:k + 1], fin[:, i, :], ALU.mult, ALU.add)
                    last.then_inc(sem("combine_step" if k == 2 else "combined"), 1)
                    if i > 0 and k == 2:
                        if i == 1:
                            dve.wait_ge(sem("g_final_landed"), 16)
                        scaled(i - 1)
            scaled(NT - 1)


_INS = ["x", "meta_tokens", "lb_logits", "g_mix", "w_in", "w_dw", "b_dw", "ln_g", "ln_b", "w_conv_out",
        "b_conv_out", "g_onorm", "w_rnn_out", "w_o", "g_ffn", "w_router", "b_router", "w_gate_up",
        "b_gate_up", "w_down", "b_down", "g_final"]
_OUTS = [((1, SEQ, D), "float32")]


def kernel(**inputs):
    import numpy as _np
    import concourse.bacc as _bacc
    from concourse import mybir as _mybir
    from concourse.bass_utils import run_bass_kernel_spmd as _run

    nc = _bacc.Bacc("TRN2", target_bir_lowering=False, num_devices=1)
    arrays, args = {}, []
    for name in _INS:
        a = _np.ascontiguousarray(inputs[name])
        arrays[f"in_{name}_dram"] = a
        args.append(nc.dram_tensor(f"in_{name}_dram", a.shape, _mybir.dt.from_np(a.dtype), kind="ExternalInput").ap())
    for i, (shape, dtype) in enumerate(_OUTS):
        dt = _mybir.dt.from_np(_np.dtype(dtype))
        args.append(nc.dram_tensor(f"out_{i}_dram", shape, dt, kind="ExternalOutput").ap())
    hybrid_block(nc, *args)
    r = _run(nc, [arrays], core_ids=[0])
    return r.results[0]["out_0_dram"]
```
